# Optimizing a Trainium2 kernel written in Bass

```python
import math
import jax, jax.numpy as jnp
from jax import lax
import numpy as np

D_MODEL = 2048
BATCH = 1
SEQ = 256
DEPTH = 1

A_HEADS = 16
A_HEAD_DIM = 128
A_PATTERNS = ((128, 1), (512, 4), (2048, 16))
A_BLOCK = 128
A_WIDTH = A_HEADS * A_HEAD_DIM
B_HEADS = 16
Q_LORA = 512
KV_LORA = 512
QK_NOPE = 128
QK_ROPE = 64
V_HEAD = 128
ROPE_THETA = 10000.0
Q_BLOCK = 128
N_KEYS = 128
N_EXPERTS = N_KEYS * N_KEYS
PEER_HEADS = 8
PEER_QDIM = 256
PEER_TOPK = 16
PEER_CHUNK = 128
LN_EPS = 1e-5
RMS_EPS = 1e-6
ALPHA = (2.0 * DEPTH) ** 0.25
BETA = (8.0 * DEPTH) ** -0.25
NEG = -1e30
IN_SIZES = (A_WIDTH, A_WIDTH, A_WIDTH, Q_LORA, KV_LORA, QK_ROPE, 2 * D_MODEL)
IN_WIDTH = sum(IN_SIZES)
IN_SPLITS = tuple(int(v) for v in np.cumsum(IN_SIZES)[:-1])

kernel_name = 'hybrid_dilated_mla_peer_deepnorm'

def layer_norm(x, g, b):
    xf = x.astype(jnp.float32)
    mu = jnp.mean(xf, axis=-1, keepdims=True)
    var = jnp.mean(jnp.square(xf - mu), axis=-1, keepdims=True)
    return ((xf - mu) * lax.rsqrt(var + LN_EPS) * g + b).astype(x.dtype)

def rms_norm(x, g):
    xf = x.astype(jnp.float32)
    ms = jnp.mean(jnp.square(xf), axis=-1, keepdims=True)
    return (xf * lax.rsqrt(ms + RMS_EPS) * g).astype(x.dtype)

def apply_rope(t, positions):
    half = t.shape[-1] // 2
    inv_freq = ROPE_THETA ** (-jnp.arange(half, dtype=jnp.float32) / half)
    ang = positions.astype(jnp.float32)[:, None] * inv_freq[None, :]
    cos = jnp.cos(ang)[:, None, :].astype(t.dtype)
    sin = jnp.sin(ang)[:, None, :].astype(t.dtype)
    t1, t2 = t[..., :half], t[..., half:]
    return jnp.concatenate([t1 * cos - t2 * sin, t1 * sin + t2 * cos], axis=-1)

def alibi_slopes(n_heads):
    return jnp.power(2.0, -8.0 * jnp.arange(1, n_heads + 1, dtype=jnp.float32) / n_heads)

def dilated_window_attention(q, k, v, window, dilation, slopes):
    B, S, H, Dh = q.shape
    steps = window // dilation
    L = S // dilation
    nb = -(-L // A_BLOCK)
    Lp = nb * A_BLOCK

    def to_sub(t):
        t = t.reshape(B, L, dilation, H, Dh).transpose(0, 2, 3, 1, 4)
        t = jnp.pad(t, ((0, 0), (0, 0), (0, 0), (0, Lp - L), (0, 0)))
        return t.reshape(B, dilation, H, nb, A_BLOCK, Dh)

    def with_prev(t):
        prev = jnp.pad(t, ((0, 0), (0, 0), (0, 0), (1, 0), (0, 0), (0, 0)))[:, :, :, :-1]
        return jnp.concatenate([prev, t], axis=4)

    qb = to_sub(q)
    kw = with_prev(to_sub(k))
    vw = with_prev(to_sub(v))
    s = jnp.einsum('bdhnqc,bdhnkc->bdhnqk', qb, kw).astype(jnp.float32) * (Dh ** -0.5)

    i = jnp.arange(A_BLOCK)[:, None]
    c = jnp.arange(2 * A_BLOCK)[None, :]
    rel = A_BLOCK + i - c
    band = (rel >= 0) & (rel <= steps)
    blk = jnp.arange(nb)[:, None, None]
    valid = band[None] & (blk * A_BLOCK + c[None] >= A_BLOCK)
    bias = -slopes[:, None, None] * (dilation * rel).astype(jnp.float32)
    logits = jnp.where(valid, s + bias[None, None, :, None], NEG)

    m = jnp.max(logits, axis=-1, keepdims=True)
    p = jnp.exp(logits - m)
    z = jnp.sum(p, axis=-1, keepdims=True)
    o = jnp.einsum('bdhnqk,bdhnkc->bdhnqc', p / z, vw).astype(q.dtype)
    lse = (m + jnp.log(z))[..., 0]

    o = o.reshape(B, dilation, H, Lp, Dh)[:, :, :, :L].transpose(0, 3, 1, 2, 4).reshape(B, S, H, Dh)
    lse = lse.reshape(B, dilation, H, Lp)[:, :, :, :L].transpose(0, 3, 1, 2).reshape(B, S, H)
    return o, lse

def mla_attention(q_nope, q_rope, k_nope, k_rope, v):
    B, S, H, _ = q_nope.shape
    nq = S // Q_BLOCK
    scale = (QK_NOPE + QK_ROPE) ** -0.5
    kpos = jnp.arange(S)

    def block(args):
        qn, qr, start = args
        s = (jnp.einsum('bqhc,bkhc->bhqk', qn, k_nope)
             + jnp.einsum('bqhr,bkr->bhqk', qr, k_rope)).astype(jnp.float32) * scale
        qpos = start + jnp.arange(Q_BLOCK)
        s = jnp.where(kpos[None, :] <= qpos[:, None], s, NEG)
        p = jax.nn.softmax(s, axis=-1)
        return jnp.einsum('bhqk,bkhc->bqhc', p, v).astype(v.dtype)

    qn_b = q_nope.reshape(B, nq, Q_BLOCK, H, QK_NOPE).transpose(1, 0, 2, 3, 4)
    qr_b = q_rope.reshape(B, nq, Q_BLOCK, H, QK_ROPE).transpose(1, 0, 2, 3, 4)
    starts = jnp.arange(nq, dtype=jnp.int32) * Q_BLOCK
    out = lax.map(block, (qn_b, qr_b, starts))
    return out.transpose(1, 0, 2, 3, 4).reshape(B, S, H, V_HEAD)

def peer(x, w_query, sub_keys_1, sub_keys_2, expert_down, expert_up):
    B, S, D = x.shape
    q = (x @ w_query).reshape(B, S, PEER_HEADS, 2, PEER_QDIM // 2)
    s1 = jnp.einsum('bshc,kc->bshk', q[..., 0, :], sub_keys_1).astype(jnp.float32)
    s2 = jnp.einsum('bshc,kc->bshk', q[..., 1, :], sub_keys_2).astype(jnp.float32)
    v1, i1 = lax.top_k(s1, PEER_TOPK)
    v2, i2 = lax.top_k(s2, PEER_TOPK)
    cand_s = (v1[..., :, None] + v2[..., None, :]).reshape(B, S, PEER_HEADS, PEER_TOPK * PEER_TOPK)
    cand_i = (i1[..., :, None] * N_KEYS + i2[..., None, :]).reshape(B, S, PEER_HEADS, PEER_TOPK * PEER_TOPK)
    top_s, pos = lax.top_k(cand_s, PEER_TOPK)
    expert_idx = jnp.take_along_axis(cand_i, pos, axis=-1)
    gates = jax.nn.softmax(top_s, axis=-1)

    T = B * S
    nc = T // PEER_CHUNK
    E = PEER_HEADS * PEER_TOPK
    xc = x.reshape(nc, PEER_CHUNK, D)
    ec = expert_idx.reshape(nc, PEER_CHUNK, E)
    gc = gates.reshape(nc, PEER_CHUNK, E).astype(x.dtype)

    def chunk(args):
        xt, et, gt = args
        u = expert_down[et]
        h = jax.nn.gelu(jnp.einsum('cd,ced->ce', xt, u), approximate=False)
        vv = expert_up[et]
        return jnp.einsum('ce,ced->cd', gt * h, vv)

    y = lax.map(chunk, (xc, ec, gc))
    return y.reshape(B, S, D)

def setup_inputs(seed: int = 0) -> dict:
    key = jax.random.key(seed)
    ks = jax.random.split(key, 24)
    f32 = jnp.float32

    def normal(k, shape, scale):
        return jax.random.normal(k, shape, f32) * scale

    x = normal(ks[0], (BATCH, SEQ, D_MODEL), 1.0)
    in_scale = jnp.concatenate([jnp.ones((2 * A_WIDTH,), f32), jnp.full((A_WIDTH,), BETA, f32),
                                jnp.ones((IN_WIDTH - 3 * A_WIDTH,), f32)])
    w_in = normal(ks[1], (DEPTH, D_MODEL, IN_WIDTH), D_MODEL ** -0.5) * in_scale
    b_gates = normal(ks[2], (DEPTH, 2 * D_MODEL), 0.02)
    a_w_out = normal(ks[3], (DEPTH, A_WIDTH, D_MODEL), A_WIDTH ** -0.5)
    mla_q_norm = 1.0 + normal(ks[4], (DEPTH, Q_LORA), 0.02)
    mla_w_uq = normal(ks[5], (DEPTH, Q_LORA, B_HEADS * (QK_NOPE + QK_ROPE)), Q_LORA ** -0.5)
    mla_kv_norm = 1.0 + normal(ks[6], (DEPTH, KV_LORA), 0.02)
    ukv_scale = jnp.concatenate([jnp.ones((QK_NOPE,), f32), jnp.full((V_HEAD,), BETA, f32)])
    mla_w_ukv = (normal(ks[7], (DEPTH, KV_LORA, B_HEADS, QK_NOPE + V_HEAD), KV_LORA ** -0.5)
                 * ukv_scale).reshape(DEPTH, KV_LORA, B_HEADS * (QK_NOPE + V_HEAD))
    mla_w_out = normal(ks[8], (DEPTH, B_HEADS * V_HEAD, D_MODEL), (B_HEADS * V_HEAD) ** -0.5)
    w_out = normal(ks[9], (DEPTH, D_MODEL, D_MODEL), BETA * D_MODEL ** -0.5)
    ln1_g = 1.0 + normal(ks[10], (DEPTH, D_MODEL), 0.02)
    ln1_b = normal(ks[11], (DEPTH, D_MODEL), 0.02)
    peer_w_query = normal(ks[12], (DEPTH, D_MODEL, PEER_HEADS * PEER_QDIM), D_MODEL ** -0.5)
    peer_sub_keys_1 = normal(ks[13], (DEPTH, N_KEYS, PEER_QDIM // 2), (PEER_QDIM // 2) ** -0.5)
    peer_sub_keys_2 = normal(ks[14], (DEPTH, N_KEYS, PEER_QDIM // 2), (PEER_QDIM // 2) ** -0.5)
    peer_expert_down = normal(ks[15], (DEPTH, N_EXPERTS, D_MODEL), D_MODEL ** -0.5)
    peer_expert_up = normal(ks[16], (DEPTH, N_EXPERTS, D_MODEL), BETA)
    ln2_g = 1.0 + normal(ks[17], (DEPTH, D_MODEL), 0.02)
    ln2_b = normal(ks[18], (DEPTH, D_MODEL), 0.02)
    return {'x': x, 'w_in': w_in, 'b_gates': b_gates, 'a_w_out': a_w_out,
            'mla_q_norm': mla_q_norm, 'mla_w_uq': mla_w_uq, 'mla_kv_norm': mla_kv_norm,
            'mla_w_ukv': mla_w_ukv, 'mla_w_out': mla_w_out, 'w_out': w_out,
            'ln1_g': ln1_g, 'ln1_b': ln1_b, 'peer_w_query': peer_w_query,
            'peer_sub_keys_1': peer_sub_keys_1, 'peer_sub_keys_2': peer_sub_keys_2,
            'peer_expert_down': peer_expert_down, 'peer_expert_up': peer_expert_up,
            'ln2_g': ln2_g, 'ln2_b': ln2_b}

def reference(x, w_in, b_gates, a_w_out, mla_q_norm, mla_w_uq, mla_kv_norm, mla_w_ukv,
              mla_w_out, w_out, ln1_g, ln1_b, peer_w_query, peer_sub_keys_1, peer_sub_keys_2,
              peer_expert_down, peer_expert_up, ln2_g, ln2_b):
    B, S, D = x.shape
    positions = jnp.arange(S, dtype=jnp.int32)
    slopes = alibi_slopes(A_HEADS)
    h = x
    for l in range(DEPTH):
        proj = h @ w_in[l]
        qa, ka, va, cq, ckv, kr, gate_pre = jnp.split(proj, IN_SPLITS, axis=-1)
        gates = jax.nn.sigmoid(gate_pre + b_gates[l])
        g_a, g_b = gates[..., :D_MODEL], gates[..., D_MODEL:]

        qa = qa.reshape(B, S, A_HEADS, A_HEAD_DIM)
        ka = ka.reshape(B, S, A_HEADS, A_HEAD_DIM)
        va = va.reshape(B, S, A_HEADS, A_HEAD_DIM)
        outs, lses = [], []
        for window, dilation in A_PATTERNS:
            o_g, lse_g = dilated_window_attention(qa, ka, va, window, dilation, slopes)
            outs.append(o_g)
            lses.append(lse_g)
        w_pat = jax.nn.softmax(jnp.stack(lses, axis=0), axis=0).astype(h.dtype)
        y_a = jnp.einsum('gbsh,gbshc->bshc', w_pat, jnp.stack(outs, axis=0)).reshape(B, S, A_WIDTH)
        y_a = y_a @ a_w_out[l]

        cq = rms_norm(cq, mla_q_norm[l])
        q_b = (cq @ mla_w_uq[l]).reshape(B, S, B_HEADS, QK_NOPE + QK_ROPE)
        q_nope = q_b[..., :QK_NOPE]
        q_rope = apply_rope(q_b[..., QK_NOPE:], positions)
        ckv = rms_norm(ckv, mla_kv_norm[l])
        kv = (ckv @ mla_w_ukv[l]).reshape(B, S, B_HEADS, QK_NOPE + V_HEAD)
        k_nope, v_b = kv[..., :QK_NOPE], kv[..., QK_NOPE:]
        k_rope = apply_rope(kr[:, :, None, :], positions)[:, :, 0]
        y_b = mla_attention(q_nope, q_rope, k_nope, k_rope, v_b).reshape(B, S, B_HEADS * V_HEAD)
        y_b = y_b @ mla_w_out[l]

        mix = (g_a * y_a + g_b * y_b) @ w_out[l]
        h = layer_norm(ALPHA * h + mix, ln1_g[l], ln1_b[l])

        y_p = peer(h, peer_w_query[l], peer_sub_keys_1[l], peer_sub_keys_2[l],
                   peer_expert_down[l], peer_expert_up[l])
        h = layer_norm(ALPHA * h + y_p, ln2_g[l], ln2_b[l])
    return h


_drawn_inputs = setup_inputs


def setup_inputs(seed=0):
    import zlib

    import numpy as np

    out = dict(_drawn_inputs(seed))
    spreads = {}
    factors = {'b_gates': 8.0, 'mla_q_norm': 8.0, 'mla_kv_norm': 8.0, 'ln2_g': 2.827, 'ln2_b': 2.842}
    for name, (base, spread) in spreads.items():
        noise = np.random.default_rng([zlib.crc32(name.encode()), seed]).standard_normal(out[name].shape)
        drawn = base * np.exp(spread * noise) if base else spread * noise
        out[name] = __import__('jax').numpy.asarray(drawn.astype(out[name].dtype))
    for name, factor in factors.items():
        out[name] = (out[name] * factor).astype(out[name].dtype)
    return out
```

```python
import math
from contextlib import ExitStack

import numpy as np

import concourse.bass as bass
from concourse import mybir

F32 = mybir.dt.float32
F32R = mybir.dt.float32r
U32 = mybir.dt.uint32
ALU = mybir.AluOpType
ACT = mybir.ActivationFunctionType
AX_X = mybir.AxisListType.X

P = 128
T = 256
TT = T // P
D = 2048
KD = D // P
HEADS = 16
LORA = 512
KL = LORA // P
ROPE = 64
NOPE = 128
NKEYS = 128
PEER_HEADS = 8
TOPK = 16
SLOTS = PEER_HEADS * TOPK
LN_EPS = 1e-5
RMS_EPS = 1e-6
ALPHA = 2.0 ** 0.25
NEG = -1e30
SCALE_A = 128 ** -0.5
SCALE_B = (NOPE + ROPE) ** -0.5
PATTERNS = ((128, 1), (512, 4), (2048, 16))

T_QKVG = 0
T_LAT = T_QKVG + 4 * HEADS
T_GB = T_LAT + 2 * KL + 1
T_MLA = T_GB + KD
T_MO = T_MLA + 2 * HEADS
T_WO = T_MO + KD
T_WQ = T_WO + KD
T_DN = T_WQ + KD
T_UP = T_DN + NKEYS
N_TILES = T_UP + NKEYS
HALF = 1024
ROUNDS_TOP = 6
ROUNDS_REST = 2
TOP_TILES = 3

C_D, C_NA, C_NB, C_C = 0, 384, 768, 1152
C_ROPE = 1536
C_ID = C_ROPE + T
C_ONE = C_ID + P
C_IOTA = C_ONE + P
C_SLOPE = C_IOTA + P
N_CONST = C_SLOPE + HEADS
S_BG, S_QN, S_KN, S_G1, S_B1 = 0, 2 * KD, 2 * KD + KL, 2 * KD + 2 * KL, 3 * KD + 2 * KL
N_SMALL = 4 * KD + 2 * KL


class Tile:

    def __init__(self, const, i=0, step=0):
        self.const, self.i, self.step = const, i, step
        self.par = const % 2
        self.n = i * step + const if step else const
        self.pair = i * (step // 2) + const // 2 if step else const // 2

    def next(self):
        return Tile(self.const + 1, self.i, self.step)

    def half(self, hf):
        return self.n * 2 + hf

    def slot(self, hf):
        return 2 * self.par + hf


class Chain:

    def __init__(self, eng, sem):
        self.eng, self.sem, self.base, self.k = eng, sem, 0, 0

    def link(self, ins):
        ins.then_inc(self.sem, 1)
        self.k += 1
        self.eng.wait_ge(self.sem, self.base + self.k)

    def enter(self, i, per, first=0):
        self.outer = self.base + self.k
        self.per = per
        self.base, self.k = i * per + (self.outer - first * per), 0

    def leave(self, rounds):
        assert self.k == self.per, (self.k, self.per)
        self.base, self.k = self.outer + rounds * self.per, 0


def build(nc, stream, x_t, const_in, small_in, keys_t, ln2, y_out, a_dram, g_dram):
    ctx = ExitStack()

    def sb(name, shape, dt=F32, stack=ctx):
        return stack.enter_context(nc.sbuf_tensor(name, shape, dt))

    def sem(name):
        return ctx.enter_context(nc.semaphore(name))

    raw = sb("raw", [P, 4, HALF])
    w_hi = sb("w_hi", [P, 4, HALF], F32R)
    w_lo = sb("w_lo", [P, 4, HALF], F32R)
    a_hi = sb("a_hi", [P, KD, T], F32R)
    a_lo = sb("a_lo", [P, KD, T], F32R)
    res = sb("res", [P, KD, T])
    cst = sb("cst", [P, N_CONST])
    small = sb("small", [P, N_SMALL])
    stat = sb("stat", [P, 16])
    carrier = sb("carrier", [P, 1])
    mix_mem = ExitStack()
    b_hi = sb("b_hi", [P, KD, T], F32R, mix_mem)
    b_lo = sb("b_lo", [P, KD, T], F32R, mix_mem)
    gate_a = sb("gate_a", [P, KD, T], F32, mix_mem)
    gate_b = sb("gate_b", [P, KD, T], F32, mix_mem)
    lat = sb("lat", [P, 2 * KL, T], F32, mix_mem)
    c_hi = sb("c_hi", [P, 2 * KL, T], F32R, mix_mem)
    c_lo = sb("c_lo", [P, 2 * KL, T], F32R, mix_mem)
    logit = sb("logit", [P, 384], F32, mix_mem)
    p_t = sb("p_t", [P, 384], F32, mix_mem)
    head = sb("head", [P, 4, T], F32, mix_mem)
    kr_s = sb("kr_s", [ROPE, T], F32, mix_mem)
    v_t = sb("v_t", [P, T], F32, mix_mem)
    rot = sb("rot", [ROPE, 2, T], F32, mix_mem)
    wide = sb("wide", [P, T], F32, mix_mem)
    mean_s = sb("mean_s", [P, T], F32, mix_mem)
    mix_mem.close()
    peer_mem = ExitStack()
    h1_n = sb("h1_n", [P, TT, D], F32, peer_mem)
    ln2_s = sb("ln2_s", [P, 2, D], F32, peer_mem)
    down_mem = ExitStack()
    sc = sb("sc", [P, TT, 2 * PEER_HEADS, NKEYS], F32, down_mem)
    oh1 = sb("oh1", [P, 2, 4, NKEYS], F32, down_mem)
    oh2 = sb("oh2", [P, 2, 4, NKEYS], F32, down_mem)
    qp = sb("qp", [P, KD, T], F32, down_mem)
    keys = sb("keys", [P, 2, NKEYS], F32, down_mem)
    act4 = sb("act4", [P, 2, 4, T], F32, down_mem)
    work = sb("work", [P, TOPK * TOPK], F32, down_mem)
    cand = sb("cand", [P, TOPK * TOPK], F32, down_mem)
    pick = sb("pick", [P, TOPK, TOPK], F32, down_mem)
    val = sb("val", [P, 3, TOPK], F32, down_mem)
    idx = sb("idx", [P, 3, TOPK], U32, down_mem)
    idx2 = sb("idx2", [P, 2, TOPK], U32, down_mem)
    idx_f = sb("idx_f", [P, 4, TOPK], F32, down_mem)
    slot = sb("slot", [P, 3, TT, SLOTS], F32, down_mem)
    slot_t = sb("slot_t", [P, 3, T], F32, down_mem)
    down_mem.close()
    up_mem = ExitStack()
    a_in = sb("a_in", [P, 2, 4, T], F32, up_mem)
    g_in = sb("g_in", [P, 2, 8, 4, 32], F32, up_mem)
    m_f = sb("m_f", [P, 2, T], F32, up_mem)
    m_hi = sb("m_hi", [P, 2, T], F32R, up_mem)
    m_lo = sb("m_lo", [P, 2, T], F32R, up_mem)
    zero = sb("zero", [P, 512], mybir.dt.bfloat16, up_mem)
    y_s = sb("y_s", [P, TT, D], F32, up_mem)
    bn = sb("bn", [P, TT, 4, 6], F32, up_mem)
    bn2 = sb("bn2", [P, TT, 2], F32, up_mem)
    up_mem.close()
    peer_mem.close()

    ps = ctx.enter_context(nc.psum_tensor("ps", [P, 8 * 512], F32))
    acc = [ps[:, 0:1024], ps[:, 1024:2048]]
    ps_s = ps[:, 2048:2560]
    ps_p = ps[:, 2560:3072]
    ps_o = ps[:, 3072:3584]
    ps_m = ps[:, 3584:4096]
    spare = [ps_s, ps_p, ps_o, ps_m]

    raw_in = [sem(f"raw_in{s}") for s in range(4)]
    hi_ready, lo_ready, half_used = sem("hi_ready"), sem("lo_ready"), sem("half_used")
    acc_free = [sem("acc_free0"), sem("acc_free1")]
    x_in, par_in, keys_in, ln2_in = [sem(f"x_in{q}") for q in range(4)], sem("par_in"), sem("keys_in"), sem("ln2_in")
    par_in2 = sem("par_in2")
    x_hi, x_lo, vt_ready, vt_mm, v_ready = sem("x_hi"), sem("x_lo"), sem("vt_ready"), sem("vt_mm"), sem("v_ready")
    eps_ok, sum_ready, u_ready = sem("eps_ok"), sem("sum_ready"), sem("u_ready")
    ev_q, ev_v = sem("ev_q"), sem("ev_v")
    s_ready, max_ready, p_ready, pn_ready = sem("s_ready"), sem("max_ready"), sem("p_ready"), sem("pn_ready")
    pt_ready, pts_ready, o_ready, o_hi, o_lo = sem("pt_ready"), sem("pts_ready"), sem("o_ready"), sem("o_hi"), sem("o_lo")
    sq_ready, ms_ready, var_ready, std_ready = sem("sq_ready"), sem("ms_ready"), sem("var_ready"), sem("std_ready")
    cn_ready, c_hi_r, c_lo_r, kr_ready, rope_q = sem("cn_ready"), sem("c_hi_r"), sem("c_lo_r"), sem("kr_ready"), sem("rope_q")
    mix_f, mix_hi, mix_lo = sem("mix_f"), sem("mix_hi"), sem("mix_lo")
    r_ready, mean_ready, cen_ready, csq_ready, cvar_ready = sem("r_ready"), sem("mean_ready"), sem("cen_ready"), sem("csq_ready"), sem("cvar_ready")
    h1_ready, h1_hi, h1_lo = sem("h1_ready"), sem("h1_hi"), sem("h1_lo")
    sc_mm, sc_ready, ht_mm, ht_ready = sem("sc_mm"), sem("sc_ready"), sem("ht_mm"), sem("ht_ready")
    a_out = [sem("a_out0"), sem("a_out1")]
    act4_free, g_blk_free = [sem("act4_free0"), sem("act4_free1")], [sem("g_blk_free0"), sem("g_blk_free1")]
    top_ready, gexp_ready, slots_ready, st_mm, st_ready = sem("top_ready"), sem("gexp_ready"), sem("slots_ready"), sem("st_mm"), sem("st_ready")
    oh_ready, g_mm, g_sb, g_out = sem("oh_ready"), sem("g_mm"), sem("g_sb"), [sem("g_out0"), sem("g_out1")]
    ag_in = [sem("ag_in0"), sem("ag_in1")]
    m_ready, mhi_ready, mlo_ready, y_ready = sem("m_ready"), sem("mhi_ready"), sem("mlo_ready"), sem("y_ready")
    g_ready = sem("g_ready")
    z_ready, mv_ready, sd_ready, nb_ready, ln_ready, out_ready, y_done = (
        sem("z_ready"), sem("mv_ready"), sem("sd_ready"), sem("nb_ready"), sem("ln_ready"), sem("out_ready"), sem("y_done"))
    dve_step, act_step = sem("dve_step"), sem("act_step")

    run = head[:, 0:2, :]
    q_s, k_s, qr_s = head[:, 0, :], head[:, 1, :], head[0:ROPE, 3, :]
    v_s = head[:, 2, :].rearrange("p (b n) -> p b n", b=TT)
    g_view = g_dram.rearrange("g p (q x) -> q p g x", x=4 * 32)
    rstd = (wide, mean_s)

    def col(c, n):
        return cst[:, c:c + n]

    def one(h):
        return bass.ds(h, 1)

    ident = col(C_ID, P)
    ones = col(C_ONE, P)
    iota = col(C_IOTA, P)
    g_flat = (sc[:].rearrange("p a b n -> p (a b n)"), qp[:].rearrange("p k t -> p (k t)"))
    g_blk = [g.rearrange("p (j t) -> p j t", t=32) for g in g_flat]
    block = ctx.enter_context(nc.Block())

    HALVES_FREE = 4

    @block.sync
    def _(sp):
        with sp.Fori(0, N_TILES // 2) as i:
            for s in range(4):
                sp.wait_ge(lo_ready, i * 4 + (s + 1))
                sp.dma_start(raw[:, s, :], stream[i * 4 + s]).then_inc(raw_in[s], 16)
        for s in range(2 * (N_TILES % 2)):
            h = N_TILES // 2 * 4 + s
            sp.wait_ge(lo_ready, h + 1)
            sp.dma_start(raw[:, s, :], stream[h]).then_inc(raw_in[s], 16)
        for tt in range(TT):
            for c in range(4):
                o = slice(512 * c, 512 * c + 512)
                sp.wait_ge(out_ready, 4 * tt + c + 1)
                sp.dma_start(y_out[tt][:, o], y_s[:, tt, o]).then_inc(y_done, 16)
        sp.wait_ge(y_done, 16 * 4 * TT)

    @block.gpsimd
    def _(pool):
        pool.wait_ge(x_in[3], 16)
        pool.dma_start(small[:], small_in).then_inc(par_in, 16)
        pool.dma_start(cst[:], const_in).then_inc(par_in2, 16)
        for b in range(2):
            pool.sem_inc(g_blk_free[b], 1)
            pool.sem_inc(act4_free[b], 1)
        for k in range(KD):
            pool.wait_ge(h1_lo, k // 4 + 1)
            ins = pool.tensor_scalar(res[:, k, :], res[:, k, :], small[:, S_B1 + k:S_B1 + k + 1], None, ALU.add)
            ins.then_inc(h1_ready, 1)
        pool.wait_ge(h1_lo, 4)
        pool.dma_start(keys[:], keys_t).then_inc(keys_in, 16)
        pool.dma_start(ln2_s[:], ln2.partition_broadcast(P)).then_inc(ln2_in, 16)

        def store(b, rnd):
            t = Tile(T_DN + 4 * b + 3, rnd, 8) if not isinstance(rnd, int) else Tile(T_DN + 4 * b + 3 + 8 * rnd)
            pool.wait_ge(acc_free[t.par], t.pair + 2)
            pool.dma_start(a_dram[rnd * 2 + b], act4[:, b, :, :]).then_inc(a_out[b], 16)

        def stored(b, rnd):
            pool.wait_ge(a_out[b], rnd * 16 + 16)
            pool.sem_inc(act4_free[b], 1)

        def both_stores(rnd):
            store(0, rnd)
            stored(0, rnd)
            store(1, rnd)
            stored(1, rnd)

        def loads(i, b):
            pool.dma_start(a_in[:, b], a_dram[i * 2 + b]).then_inc(ag_in[b], 16)
            pool.dma_start(g_in[:, b].rearrange("p g j t -> p g (j t)"), g_view[i * 2 + b]).then_inc(ag_in[b], 16)

        with pool.Fori(0, ROUNDS_TOP) as i:
            both_stores(i)
        with pool.Fori(0, TT * P // 64) as i:
            for g in range(2):
                both_stores(i * 2 + (ROUNDS_TOP + g))
                pool.wait_ge(g_sb, i * 16 + (8 * g + 9))
                pool.dma_start(g_dram[i * 2 + g], g_flat[g]).then_inc(g_out[g], 16)
                pool.wait_ge(g_out[g], i * 16 + 16)
                pool.sem_inc(g_blk_free[g], 1)
        for b in range(2):
            loads(0, b)
        for r in range(ROUNDS_REST):
            both_stores(NKEYS // 8 - ROUNDS_REST + r)
        with pool.Fori(1, NKEYS // 8) as i:
            for b in range(2):
                pool.wait_ge(m_ready, i * 8 + (4 * b + 4))
                loads(i, b)
        pool.wait_ge(ln2_in, 16)
        for tt in range(TT):
            for c in range(4):
                o = slice(512 * c, 512 * c + 512)
                pool.wait_ge(g_ready, 4 * tt + c + 1)
                pool.tensor_tensor(y_s[:, tt, o], y_s[:, tt, o], ln2_s[:, 1, o], ALU.add).then_inc(out_ready, 1)

    @block.scalar
    def _(act):
        for q in range(4):
            act.dma_start(res[:, 4 * q:4 * q + 4, :], x_t[:, 4 * q:4 * q + 4, :]).then_inc(x_in[q], 16)
        for b in range(2):
            act.sem_inc(acc_free[b], 1)
        act.sem_inc(g_sb, 1)

        def hi(t):
            for hf in range(2):
                act.wait_ge(raw_in[t.slot(hf)], t.pair * 16 + 16)
                act.wait_ge(half_used, t.half(hf) + 1)
                act.activation(w_hi[:, t.slot(hf), :], raw[:, t.slot(hf), :], ACT.Copy).then_inc(hi_ready, 1)

        def done(t):
            act.wait_ge(half_used, t.half(1) + 1 + HALVES_FREE)

        def exps(a, with_sum):
            act.wait_ge(max_ready, a + 1)
            z = {"accum_out": stat[:, 2:3]} if with_sum else {}
            act.activation(logit[:, 0:128], logit[:, 0:128], ACT.Exp, bias=stat[:, 0:1], **z)
            z = {"accum_out": stat[:, 3:4]} if with_sum else {}
            act.activation(logit[:, 128:384], logit[:, 128:384], ACT.Exp, bias=stat[:, 1:2], **z).then_inc(p_ready, 1)

        def pt_copy(a):
            act.wait_ge(pt_ready, a + 1)
            act.activation(p_t[:], ps_p[:, 0:384], ACT.Copy).then_inc(pts_ready, 1)

        def out_hi(a, dst):
            act.wait_ge(o_ready, a + 1)
            act.activation(dst, ps_o[:, 0:T], ACT.Copy).then_inc(o_hi, 1)

        for q in range(4):
            act.wait_ge(x_in[q], 16)
            act.activation(a_hi[:, 4 * q:4 * q + 4, :], res[:, 4 * q:4 * q + 4, :], ACT.Copy).then_inc(x_hi, 1)
        hi(Tile(0))
        act.wait_ge(par_in, 16)

        def v_copy(a):
            act.wait_ge(vt_mm, a + 1)
            act.activation(v_s, ps_m[:, 0:T].rearrange("p (b n) -> p b n", b=TT), ACT.Copy).then_inc(v_ready, 1)

        def head_a(h, first):
            t = Tile(T_QKVG, h, 4) if not first else Tile(0)
            hi(t.next())
            done(t)
            act.activation(q_s, acc[t.par][:, 0:T], ACT.Copy).then_inc(acc_free[t.par], 1)
            t = t.next()
            hi(t.next())
            if not first:
                pt_copy(h - 1)
            done(t)
            act.activation(k_s, acc[t.par][:, 0:T], ACT.Copy).then_inc(acc_free[t.par], 1)
            t = t.next()
            hi(t.next())
            if not first:
                out_hi(h - 1, b_hi[:, h - 1, :])
            done(t)
            act.activation(v_t[:], acc[t.par][:, 0:T], ACT.Copy).then_inc(acc_free[t.par], 1)
            t = t.next()
            hi(t.next())
            exps(h, False)
            done(t)
            act.activation(gate_a[:, h, :], acc[t.par][:, 0:T], ACT.Identity, bias=small[:, one(h)]).then_inc(acc_free[t.par], 1)
            v_copy(h)

        head_a(0, True)
        with act.Fori(1, HEADS) as h:
            head_a(h, False)
        def squares(c):
            t = Tile(T_LAT + KL * c + KL - 1)
            act.wait_ge(acc_free[t.par], t.pair + 2)
            act.wait_ge(ms_ready, c) if c else None
            act.activation(head[:], lat[:, KL * c:KL * c + KL, :], ACT.Square).then_inc(sq_ready, 1)

        def norm_steps(c):
            act.wait_ge(var_ready, c + 1)
            act.activation(rstd[c][:], rstd[c][:], ACT.Sqrt).then_inc(std_ready, 1)
            act.wait_ge(cn_ready, c + 1)
            act.activation(c_hi[:, KL * c:KL * c + KL, :], lat[:, KL * c:KL * c + KL, :], ACT.Copy).then_inc(c_hi_r, 1)

        for m in range(2 * KL):
            t = Tile(T_LAT + m)
            hi(t.next())
            if m == 1:
                pt_copy(HEADS - 1)
            if m == 2:
                out_hi(HEADS - 1, b_hi[:, HEADS - 1, :])
            done(t)
            act.activation(lat[:, m, :], acc[t.par][:, 0:T], ACT.Copy).then_inc(acc_free[t.par], 1)
            if m % KL == KL - 1:
                squares(m // KL)
            if m == KL + 1:
                norm_steps(0)
        hi(Tile(T_LAT + 2 * KL + 1))
        norm_steps(1)
        for q in range(4):
            act.activation(gate_a[:, 4 * q:4 * q + 4, :], gate_a[:, 4 * q:4 * q + 4, :], ACT.Sigmoid)
        with act.Fori(0, KD // 2) as i:
            for b in range(2):
                t = Tile(T_GB + b, i, 2)
                hi(t.next())
                done(t)
                act.activation(gate_b[:, i * 2 + b, :], acc[t.par][:, 0:T], ACT.Sigmoid,
                               bias=small[:, one(i * 2 + (KD + b))]).then_inc(acc_free[t.par], 1)

        def head_b(h, first, a):
            t = Tile(T_MLA, h, 2) if not first else Tile(T_MLA)
            hi(t.next())
            if not first:
                pt_copy(a - 1)
            done(t)
            A = acc[t.par]
            act.activation(q_s, A[:, 0:T], ACT.Copy).then_inc(ev_q, 1)
            act.activation(k_s, A[:, 512:512 + T], ACT.Copy)
            act.activation(v_t[:], A[:, 768:1024], ACT.Copy).then_inc(ev_v, 1)
            t = t.next()
            hi(t.next())
            if not first:
                out_hi(a - 1, a_hi[:, h - 1, :])
            v_copy(a)
            exps(a, True)

        head_b(0, True, HEADS)
        with act.Fori(1, HEADS) as h:
            head_b(h, False, h + HEADS)
        pt_copy(2 * HEADS - 1)
        out_hi(2 * HEADS - 1, a_hi[:, HEADS - 1, :])

        with act.Fori(0, KD // 2) as i:
            for b in range(2):
                t = Tile(T_MO + b, i, 2)
                hi(t.next())
                act.wait_ge(mix_f, i * 2 + (b + 1))
                act.activation(b_hi[:, i * 2 + b, :], lat[:, b, :], ACT.Copy).then_inc(mix_hi, 1)
        with act.Fori(0, KD // 2) as i:
            for b in range(2):
                hi(Tile(T_WO + b, i, 2).next())
        for q in range(4):
            act.wait_ge(cen_ready, q + 1)
            act.activation(gate_a[:, 4 * q:4 * q + 4, :], res[:, 4 * q:4 * q + 4, :], ACT.Square).then_inc(csq_ready, 1)
        act.wait_ge(cvar_ready, 1)
        act.activation(wide[:], wide[:], ACT.Sqrt).then_inc(std_ready, 1)
        for k in range(KD):
            act.wait_ge(u_ready, k + 1)
            act.activation(a_hi[:, k, :], res[:, k, :], ACT.Identity, bias=small[:, S_B1 + k:S_B1 + k + 1]).then_inc(h1_hi, 1)
        with act.Fori(0, KD // 2) as i:
            for b in range(2):
                t = Tile(T_WQ + b, i, 2)
                hi(t.next())
                done(t)
                act.activation(qp[:, i * 2 + b, :], acc[t.par][:, 0:T], ACT.Copy).then_inc(acc_free[t.par], 1)
        for g in range(8):
            act.wait_ge(sc_mm, g + 1)
            act.activation(sc[:, g // 4, 4 * (g % 4):4 * (g % 4) + 4, :], spare[g % 4].rearrange("p (a n) -> p a n", a=4),
                           ACT.Copy).then_inc(sc_ready, 1)
        for g in range(8):
            act.wait_ge(ht_mm, g + 1)
            act.activation(h1_n[:, g // 4, 512 * (g % 4):512 * (g % 4) + 512], spare[g % 4], ACT.Copy).then_inc(ht_ready, 1)

        def m_high(n, par):
            act.wait_ge(m_ready, n + 1 + 8)
            act.activation(m_hi[:, par, :], m_f[:, par, :], ACT.Copy).then_inc(mhi_ready, 1)

        def gelu(t, b, rnd):
            done(t)
            if b % 4 == 0:
                act.wait_ge(act4_free[b // 4], rnd + 1)
            act.activation(act4[:, b // 4, b % 4, :], acc[t.par][:, 0:T], ACT.Gelu).then_inc(acc_free[t.par], 1)

        def top_exp(u):
            act.wait_ge(top_ready, u + 1)
            act.activation(val[:, 2, :], val[:, 2, :], ACT.Exp, bias=stat[:, 4:5], accum_out=stat[:, 5:6]).then_inc(gexp_ready, 1)

        with act.Fori(0, ROUNDS_TOP // 3) as i:
            for b in range(24):
                t = Tile(T_DN + b, i, 24)
                hi(t.next())
                if b % TOP_TILES == TOP_TILES - 1:
                    top_exp(i * 8 + b // TOP_TILES)
                gelu(t, b % 8, i * 3 + b // 8)
        for k in range(3):
            act.wait_ge(st_mm, k + 1)
            act.activation(slot_t[:, k, :], spare[k][:, 0:T], ACT.Copy).then_inc(st_ready, 1)
        with act.Fori(0, TT * P // 64) as i:
            for b in range(16):
                t = Tile(T_DN + 8 * ROUNDS_TOP + b, i, 16)
                hi(t.next())
                gelu(t, b % 8, i * 2 + (ROUNDS_TOP + b // 8))
                act.wait_ge(g_mm, i * 16 + (b + 1 + 2))
                if b % 8 == 0:
                    act.wait_ge(g_blk_free[b // 8], i + 1)
                q = 4 * (b % 8)
                act.activation(g_blk[b // 8][:, :, q:q + 4].rearrange("p j t -> p t j"),
                               ps_m.rearrange("p (t j) -> p t j", t=4), ACT.Copy).then_inc(g_sb, 1)
        for n in range(NKEYS - 8 * ROUNDS_REST, NKEYS):
            t = Tile(T_DN + n)
            hi(t.next())
            if n == NKEYS - 1:
                m_high(0, 0)
            gelu(t, n % 8, n // 8)

        def up_tiles(i, last):
            for b in range(8):
                t = Tile(T_UP + b, i, 8) if not last else Tile(T_UP + NKEYS - 8 + b)
                if last and b == 7:
                    break
                hi(t.next())
                n = i * 8 + b if not last else NKEYS - 8 + b
                m_high(n + 1, (b + 1) % 2)

        with act.Fori(0, NKEYS // 8 - 1) as i:
            up_tiles(i, False)
        up_tiles(0, True)
        for tt in range(TT):
            act.wait_ge(eps_ok, 1)
            act.wait_ge(mv_ready, tt + 1)
            act.activation(stat[:, 6 + tt:7 + tt], bn2[:, tt, 1:2], ACT.Sqrt, bias=stat[:, 14:15]).then_inc(sd_ready, 1)
            act.wait_ge(nb_ready, tt + 1)
            for c in range(4):
                o = slice(512 * c, 512 * c + 512)
                act.activation(y_s[:, tt, o], y_s[:, tt, o], ACT.Identity, bias=stat[:, 10 + tt:11 + tt],
                               scale=stat[:, 8 + tt:9 + tt]).then_inc(ln_ready, 1)

    @block.vector
    def _(dve):
        ch = Chain(dve, dve_step)
        link = ch.link
        dve.sem_inc(lo_ready, HALVES_FREE)
        dve.sem_inc(o_lo, 1)
        dve.sem_inc(m_ready, 8)

        def lo(t):
            for hf in range(2):
                s = t.slot(hf)
                dve.wait_ge(hi_ready, t.half(hf) + 1)
                dve.tensor_tensor(w_lo[:, s, :], raw[:, s, :], w_hi[:, s, :].bitcast(F32), ALU.subtract).then_inc(lo_ready, 1)

        def done(t):
            dve.wait_ge(half_used, t.half(1) + 1 + HALVES_FREE)

        def softmax(a, dilated, h):
            dve.wait_ge(s_ready, a + 1)
            if dilated:
                link(dve.scalar_tensor_tensor(out=logit[:], in0=col(C_D, 384), scalar=cst[:, bass.ds(h + C_SLOPE, 1)],
                                              in1=col(C_NA, 384), op0=ALU.mult, op1=ALU.add))
                link(dve.scalar_tensor_tensor(out=logit[:], in0=ps_s[:, 0:384], scalar=SCALE_A, in1=logit[:],
                                              op0=ALU.mult, op1=ALU.add))
            else:
                link(dve.scalar_tensor_tensor(out=logit[:], in0=ps_s[:, 0:384], scalar=SCALE_B, in1=col(C_NB, 384),
                                              op0=ALU.mult, op1=ALU.add))
            dve.tensor_reduce(stat[:, 0:1], logit[:, 0:128], AX_X, ALU.max, negate=True)
            dve.tensor_reduce(stat[:, 1:2], logit[:, 128:384], AX_X, ALU.max, negate=True).then_inc(max_ready, 1)
            dve.wait_ge(p_ready, a + 1)
            if dilated:
                dve.scalar_tensor_tensor(out=logit[:, 0:128], in0=logit[:, 0:128], scalar=1.0, in1=col(C_C, 128),
                                         op0=ALU.mult, op1=ALU.mult, accum_out=stat[:, 2:3])
                link(dve.scalar_tensor_tensor(out=logit[:, 128:384], in0=logit[:, 128:384], scalar=1.0, in1=col(C_C + 128, 256),
                                              op0=ALU.mult, op1=ALU.mult, accum_out=stat[:, 3:4]))
            link(dve.reciprocal(stat[:, 12:14], stat[:, 2:4]))
            dve.tensor_scalar(logit[:, 0:128], logit[:, 0:128], stat[:, 12:13], None, ALU.mult)
            dve.tensor_scalar(logit[:, 128:384], logit[:, 128:384], stat[:, 13:14], None, ALU.mult).then_inc(pn_ready, 1)

        def out_lo(a, dst, hi_part):
            dve.wait_ge(o_hi, a + 1)
            dve.tensor_tensor(dst, ps_o[:, 0:T], hi_part, ALU.subtract).then_inc(o_lo, 1)

        dve.memset(stat[:, 14:15], LN_EPS).then_inc(eps_ok, 1)
        for q in range(4):
            dve.wait_ge(x_hi, q + 1)
            dve.tensor_tensor(a_lo[:, 4 * q:4 * q + 4, :], res[:, 4 * q:4 * q + 4, :], a_hi[:, 4 * q:4 * q + 4, :].bitcast(F32),
                              ALU.subtract).then_inc(x_lo, 1)
        lo(Tile(0))
        dve.wait_ge(par_in, 16)
        dve.wait_ge(par_in2, 16)

        def head_a(h, first):
            t = Tile(T_QKVG, h, 4) if not first else Tile(0)
            lo(t.next())
            t = t.next()
            lo(t.next())
            t = t.next()
            lo(t.next())
            if not first:
                out_lo(h - 1, b_lo[:, h - 1, :], b_hi[:, h - 1, :].bitcast(F32))
            t = t.next()
            lo(t.next())
            softmax(h, True, h)

        head_a(0, True)
        with dve.Fori(1, HEADS) as h:
            ch.enter(h, 4, 1)
            head_a(h, False)
            ch.leave(HEADS - 1)
        def rotary(t, src, dst, signal, copied=None):
            done(t)
            if copied is not None:
                dve.wait_ge(ev_q, copied)
            dve.tensor_tensor(rot[:, 0, :], src[0:ROPE], col(C_ROPE, T)[0:ROPE], ALU.mult)
            if copied is not None:
                dve.wait_ge(ev_v, copied)
            dve.tensor_tensor(rot[:, 1, :], src[ROPE:P], col(C_ROPE, T)[ROPE:P], ALU.mult).then_inc(acc_free[t.par], 1)
            dve.wait_ge(acc_free[t.par], t.pair + 2)
            dve.tensor_tensor(dst, rot[:, 0, :], rot[:, 1, :], ALU.add).then_inc(signal, 1)

        def norm_steps(c):
            dve.wait_ge(ms_ready, c + 1)
            dve.tensor_scalar(rstd[c][:], (ps_m, ps_s)[c][:, 0:T], 1.0 / LORA, RMS_EPS, ALU.mult, ALU.add).then_inc(var_ready, 1)
            dve.wait_ge(std_ready, c + 1)
            link(dve.reciprocal(rstd[c][:], rstd[c][:]))
            for m in range(KL):
                ins = dve.scalar_tensor_tensor(out=lat[:, KL * c + m, :], in0=lat[:, KL * c + m, :],
                                               scalar=small[:, S_QN + KL * c + m:S_QN + KL * c + m + 1], in1=rstd[c][:],
                                               op0=ALU.mult, op1=ALU.mult)
            ins.then_inc(cn_ready, 1)
            dve.wait_ge(c_hi_r, c + 1)
            s = slice(KL * c, KL * c + KL)
            dve.tensor_tensor(c_lo[:, s, :], lat[:, s, :], c_hi[:, s, :].bitcast(F32), ALU.subtract).then_inc(c_lo_r, 1)

        for m in range(2 * KL):
            lo(Tile(T_LAT + m).next())
            if m == 2:
                out_lo(HEADS - 1, b_lo[:, HEADS - 1, :], b_hi[:, HEADS - 1, :].bitcast(F32))
            if m == KL + 1:
                norm_steps(0)
        t = Tile(T_LAT + 2 * KL)
        lo(t.next())
        norm_steps(1)
        rotary(t, acc[t.par][:, 0:T], kr_s[:], kr_ready)
        with dve.Fori(0, KD // 2) as i:
            for b in range(2):
                lo(Tile(T_GB + b, i, 2).next())

        def head_b(h, first, a):
            t = Tile(T_MLA, h, 2) if not first else Tile(T_MLA)
            lo(t.next())
            rotary(t, acc[t.par][:, T:2 * T], qr_s, rope_q, a - (HEADS - 1))
            t = t.next()
            lo(t.next())
            done(t)
            dve.tensor_tensor(gate_a[:, h, :], acc[t.par][:, 0:T], gate_a[:, h, :], ALU.mult).then_inc(acc_free[t.par], 1)
            if not first:
                out_lo(a - 1, a_lo[:, h - 1, :], a_hi[:, h - 1, :].bitcast(F32))
            softmax(a, False, h)

        head_b(0, True, HEADS)
        with dve.Fori(1, HEADS) as h:
            ch.enter(h, 2, 1)
            head_b(h, False, h + HEADS)
            ch.leave(HEADS - 1)
        out_lo(2 * HEADS - 1, a_lo[:, HEADS - 1, :], a_hi[:, HEADS - 1, :].bitcast(F32))

        with dve.Fori(0, KD // 2) as i:
            for b in range(2):
                t = Tile(T_MO + b, i, 2)
                lo(t.next())
                done(t)
                dve.tensor_tensor(gate_b[:, i * 2 + b, :], acc[t.par][:, 0:T], gate_b[:, i * 2 + b, :],
                                  ALU.mult).then_inc(acc_free[t.par], 1)
                dve.wait_ge(acc_free[t.par], t.pair + 2)
                dve.tensor_tensor(lat[:, b, :], gate_b[:, i * 2 + b, :], gate_a[:, i * 2 + b, :], ALU.add).then_inc(mix_f, 1)
                dve.wait_ge(mix_hi, i * 2 + (b + 1))
                dve.tensor_tensor(b_lo[:, i * 2 + b, :], lat[:, b, :], b_hi[:, i * 2 + b, :].bitcast(F32),
                                  ALU.subtract).then_inc(mix_lo, 1)
        dve.memset(run, 0.0)
        with dve.Fori(0, KD // 2) as i:
            for b in range(2):
                t = Tile(T_WO + b, i, 2)
                lo(t.next())
                done(t)
                dve.scalar_tensor_tensor(out=res[:, i * 2 + b, :], in0=res[:, i * 2 + b, :], scalar=ALPHA, in1=acc[t.par][:, 0:T],
                                         op0=ALU.mult, op1=ALU.add).then_inc(acc_free[t.par], 1)
                dve.wait_ge(acc_free[t.par], t.pair + 2)
                dve.tensor_tensor(run[:, b, :], run[:, b, :], res[:, i * 2 + b, :], ALU.add).then_inc(sum_ready, 1)
        dve.wait_ge(mean_ready, 1)
        link(dve.tensor_scalar(mean_s[:], ps_m[:, 0:T], 1.0 / D, None, ALU.mult))
        for q in range(4):
            s = slice(4 * q, 4 * q + 4)
            dve.tensor_tensor(res[:, s, :], res[:, s, :], mean_s[:].rearrange("p (a t) -> p a t", a=1).to_broadcast([P, 4, T]),
                              ALU.subtract).then_inc(cen_ready, 1)
        dve.wait_ge(mean_ready, 2)
        dve.tensor_scalar(wide[:], ps_s[:, 0:T], 1.0 / D, LN_EPS, ALU.mult, ALU.add).then_inc(cvar_ready, 1)
        dve.wait_ge(std_ready, 3)
        link(dve.reciprocal(wide[:], wide[:]))
        for k in range(KD + 1):
            if k < KD:
                dve.scalar_tensor_tensor(out=res[:, k, :], in0=res[:, k, :], scalar=small[:, S_G1 + k:S_G1 + k + 1],
                                         in1=wide[:], op0=ALU.mult, op1=ALU.mult).then_inc(u_ready, 1)
            if k > 0:
                dve.wait_ge(u_ready, k)
                dve.wait_ge(h1_hi, k)
                ins = dve.scalar_tensor_tensor(out=a_lo[:, k - 1, :], in0=res[:, k - 1, :], scalar=small[:, S_B1 + k - 1:S_B1 + k],
                                               in1=a_hi[:, k - 1, :].bitcast(F32), op0=ALU.add, op1=ALU.subtract)
                if k % 4 == 0:
                    ins.then_inc(h1_lo, 1)
        with dve.Fori(0, KD // 2) as i:
            for b in range(2):
                lo(Tile(T_WQ + b, i, 2).next())
        dve.wait_ge(sc_ready, 8)

        def rows(v):
            return v.rearrange("p (a o) -> p a o", o=1).to_broadcast([P, TOPK, TOPK])

        def cols(v):
            return v.rearrange("p (o b) -> p o b", o=1).to_broadcast([P, TOPK, TOPK])

        def best16(v, ix, src, rest):
            own_wait()
            link(dve.max(out=v[:, 0:8], in_=src))
            own_wait()
            dve.max_index(out=ix[:, 0:8], in_max=v[:, 0:8], in_values=src)
            link(dve.match_replace(out=rest, in_to_replace=v[:, 0:8], in_values=src, imm_value=-3e38))
            own_wait()
            link(dve.max(out=v[:, 8:16], in_=rest))
            own_wait()
            link(dve.max_index(out=ix[:, 8:16], in_max=v[:, 8:16], in_values=rest))

        def own_wait():
            dve.memset(carrier[:], 0.0)

        def top_keys(h, tt, s):
            link(dve.tensor_copy(cand[:, 0:NKEYS], sc[:, tt, h * 2 + s, :]))
            best16(val[:, s, :], idx[:, s, :], cand[:, 0:NKEYS], work[:, 0:NKEYS])

        def top_pairs():
            link(dve.tensor_tensor(cand[:].rearrange("p (a b) -> p a b", b=TOPK), rows(val[:, 0, :]), cols(val[:, 1, :]), ALU.add))
            best16(val[:, 2, :], idx[:, 2, :], cand[:], work[:])
            dve.tensor_scalar(stat[:, 4:5], val[:, 2, 0:1], -1.0, None, ALU.mult).then_inc(top_ready, 1)

        def top_experts(u, h, tt):
            dve.tensor_scalar(idx2[:, 0, :], idx[:, 2, :], 4, None, ALU.logical_shift_right)
            link(dve.tensor_scalar(idx2[:, 1, :], idx[:, 2, :], 15, None, ALU.bitwise_and))
            dve.tensor_copy(idx_f[:, 0:2, :], idx[:, 0:2, :])
            link(dve.tensor_copy(idx_f[:, 2:4, :], idx2[:]))
            for s in range(2):
                link(dve.tensor_tensor(pick[:], rows(idx_f[:, 2 + s, :]), cols(iota[:, 0:TOPK]), ALU.is_equal))
                link(dve.tensor_tensor(pick[:], pick[:], cols(idx_f[:, s, :]), ALU.mult))
                link(dve.tensor_reduce(slot[:, s, tt, bass.ds(h * TOPK, TOPK)], pick[:], AX_X, ALU.add))
            dve.wait_ge(gexp_ready, u + 1)
            link(dve.reciprocal(stat[:, 15:16], stat[:, 5:6]))
            dve.tensor_scalar(slot[:, 2, tt, bass.ds(h * TOPK, TOPK)], val[:, 2, :], stat[:, 15:16], None,
                              ALU.mult).then_inc(slots_ready, 1)
            dve.wait_ge(slots_ready, u + 1)

        with dve.Fori(0, ROUNDS_TOP // 3) as i:
            ch.enter(i, 8 * (5 + 5 + 5 + 9))
            for b in range(24):
                lo(Tile(T_DN + b, i, 24).next())
                unit = b // TOP_TILES
                h, tt = i * 4 + unit // 2, unit % 2
                if b % TOP_TILES < 2:
                    top_keys(h, tt, b % TOP_TILES)
                else:
                    top_pairs()
                    top_experts(i * 8 + unit, h, tt)
            ch.leave(ROUNDS_TOP // 3)
        dve.wait_ge(st_ready, 3)
        with dve.Fori(0, TT * P // 64) as i:
            for b in range(16):
                dve.wait_ge(g_mm, i * 16 + (b + 1))
                for q in range(4):
                    tok = i * 64 + (4 * b + q)
                    dve.tensor_scalar(oh1[:, b % 2, q, :], iota, slot_t[:, 0, bass.ds(tok, 1)], None, ALU.is_equal)
                    ins = dve.tensor_scalar(oh2[:, b % 2, q, :], iota, slot_t[:, 1, bass.ds(tok, 1)],
                                            slot_t[:, 2, bass.ds(tok, 1)], ALU.is_equal, ALU.mult)
                ins.then_inc(oh_ready, 1)
                lo(Tile(T_DN + 8 * ROUNDS_TOP + b, i, 16).next())
        for n in range(NKEYS - 8 * ROUNDS_REST, NKEYS - 1):
            lo(Tile(T_DN + n).next())
        dve.wait_ge(ag_in[0], 32)
        dve.memset(zero[:], 0.0).then_inc(z_ready, 1)

        def m_mult(n, blk, b):
            dve.wait_ge(ag_in[(b // 4) % 2], blk)
            g = g_in[:, (b // 4) % 2, :, b % 4, :]
            dve.tensor_tensor(m_f[:, b % 2, :].rearrange("p (g t) -> p g t", t=32),
                              a_in[:, (b // 4) % 2, b % 4, :].rearrange("p (g t) -> p g t", t=32), g, ALU.mult).then_inc(m_ready, 1)

        def m_low(n, par):
            dve.wait_ge(mhi_ready, n + 1)
            dve.tensor_tensor(m_lo[:, par, :], m_f[:, par, :], m_hi[:, par, :].bitcast(F32), ALU.subtract).then_inc(mlo_ready, 1)

        lo(Tile(T_UP))
        m_mult(0, 32, 0)
        m_low(0, 0)

        def up_tiles(i, last):
            for b in range(8):
                t = Tile(T_UP + b, i, 8) if not last else Tile(T_UP + NKEYS - 8 + b)
                if last and b == 7:
                    break
                lo(t.next())
                n = i * 8 + b if not last else NKEYS - 8 + b
                dve.wait_ge(half_used, t.half(0) + HALVES_FREE)
                rnd = i if not last else NKEYS // 8 - 1
                m_mult(n + 1, (rnd + (1 if b < 7 else 2)) * 32, (b + 1) % 8)
                m_low(n + 1, (b + 1) % 2)

        with dve.Fori(0, NKEYS // 8 - 1) as i:
            up_tiles(i, False)
        up_tiles(0, True)

        t = Tile(N_TILES - 1)
        done(t)
        for tt in range(TT):
            for c in range(4):
                s = slice(512 * c, 512 * c + 512)
                dve.scalar_tensor_tensor(out=y_s[:, tt, s], in0=h1_n[:, tt, s], scalar=ALPHA, in1=ps[:, 2048 * tt + 512 * c:2048 * tt + 512 * c + 512],
                                         op0=ALU.mult, op1=ALU.add).then_inc(dve_step, 1)
                ch.k += 1
            dve.wait_ge(dve_step, ch.base + ch.k)
            for c in range(4):
                ins = dve.bn_stats(bn[:, tt, c, :], y_s[:, tt, 512 * c:512 * c + 512])
            link(ins)
            dve.bn_aggr(bn2[:, tt, :], bn[:, tt, :, :]).then_inc(mv_ready, 1)
            dve.wait_ge(sd_ready, tt + 1)
            link(dve.reciprocal(stat[:, 8 + tt:9 + tt], stat[:, 6 + tt:7 + tt]))
            dve.scalar_tensor_tensor(out=stat[:, 10 + tt:11 + tt], in0=bn2[:, tt, 0:1], scalar=-1.0, in1=stat[:, 8 + tt:9 + tt],
                                     op0=ALU.mult, op1=ALU.mult).then_inc(nb_ready, 1)
        dve.wait_ge(ln2_in, 16)
        for tt in range(TT):
            for c in range(4):
                o = slice(512 * c, 512 * c + 512)
                dve.wait_ge(ln_ready, 4 * tt + c + 1)
                dve.tensor_tensor(y_s[:, tt, o], y_s[:, tt, o], ln2_s[:, 0, o], ALU.mult).then_inc(g_ready, 1)

    @block.tensor
    def _(pe):
        pe.sem_inc(half_used, HALVES_FREE)
        pe.sem_inc(g_mm, 2)

        def half_ready(t, hf):
            pe.wait_ge(lo_ready, t.half(hf) + 1 + HALVES_FREE)

        def three(out, w_slot, c0, cn, act_h, act_l, first, last):
            wh, wl = w_hi[:, w_slot, c0:c0 + cn], w_lo[:, w_slot, c0:c0 + cn]
            for q, (w, a) in enumerate(((wh, act_h), (wh, act_l), (wl, act_h))):
                ins = pe.matmul(out, w, a, start=first and q == 0, stop=last and q == 2)
            return ins

        def full(t, ah, al, part_of_act=None):
            pe.wait_ge(acc_free[t.par], t.pair + 1)
            for hf in range(2):
                half_ready(t, hf)
                for k in range(KD // 2):
                    kk = hf * (KD // 2) + k
                    if part_of_act is not None and kk % 4 == 0:
                        pe.wait_ge(part_of_act, kk // 4 + 1)
                    ins = three(acc[t.par][:, 0:T], t.slot(hf), P * k, P, ah[:, kk, :], al[:, kk, :], kk == 0, kk == KD - 1)
                ins.then_inc(half_used, 1)

        def up_proj(t):
            A = acc[t.par]
            pe.wait_ge(acc_free[t.par], t.pair + 1)
            half_ready(t, 0)
            for m in range(2):
                for k in range(KL):
                    ins = three(A[:, T * m:T * m + T], t.slot(0), LORA * m + P * k, P, c_hi[:, k, :], c_lo[:, k, :], k == 0, k == KL - 1)
            ins.then_inc(half_used, 1)
            half_ready(t, 1)
            for m in range(2):
                for k in range(KL):
                    ins = three(A[:, 512 + T * m:768 + T * m], t.slot(1), LORA * m + P * k, P, c_hi[:, KL + k, :], c_lo[:, KL + k, :],
                                k == 0, k == KL - 1)
            ins.then_inc(half_used, 1)

        def turn_v():
            for b in range(TT):
                ins = pe.transpose(ps_m[:, P * b:P * b + P], v_t[:, P * b:P * b + P], ident)
            ins.then_inc(vt_mm, 1)

        def scores(rope):
            for o, q0, k1 in ((0, 0, 128), (128, 128, 256)):
                ins = pe.matmul(ps_s[:, o:o + k1], q_s[:, q0:q0 + P], k_s[:, 0:k1], start=True, stop=not rope)
                if rope:
                    ins = pe.matmul(ps_s[:, o:o + k1], qr_s[:, q0:q0 + P], kr_s[:, 0:k1], start=False, stop=True)
            ins.then_inc(s_ready, 1)

        def transposes(a):
            pe.wait_ge(pn_ready, a + 1)
            for b in range(3):
                ins = pe.transpose(ps_p[:, P * b:P * b + P], logit[:, P * b:P * b + P], ident)
            ins.then_inc(pt_ready, 1)

        def pv(a):
            pe.wait_ge(pts_ready, a + 1)
            pe.wait_ge(v_ready, a + 1)
            pe.wait_ge(o_lo, a + 1)
            pe.matmul(ps_o[:, 0:T], v_s[:, 0, :], p_t[:, 0:T], start=True, stop=False, skip_group_check=True)
            pe.matmul(ps_o[:, P:T], v_s[:, 1, :], p_t[:, T:384], start=False, stop=True, skip_group_check=True).then_inc(o_ready, 1)

        def head_a(h, first):
            t = Tile(T_QKVG, h, 4) if not first else Tile(0)
            full(t, a_hi, a_lo, x_lo if first else None)
            if not first:
                transposes(h - 1)
            t = t.next()
            full(t, a_hi, a_lo)
            if not first:
                pv(h - 1)
            t = t.next()
            full(t, a_hi, a_lo)
            u = Tile(T_QKVG, h, 4) if not first else Tile(0)
            pe.wait_ge(acc_free[0], u.pair + 2)
            pe.wait_ge(acc_free[1], u.pair + 2)
            scores(False)
            u = t
            t = t.next()
            full(t, a_hi, a_lo)
            pe.wait_ge(acc_free[u.par], u.pair + 2)
            if first:
                pe.wait_ge(par_in2, 16)
            turn_v()

        head_a(0, True)
        with pe.Fori(1, HEADS) as h:
            head_a(h, False)
        def square_sums(c):
            pe.wait_ge(sq_ready, c + 1)
            for k in range(KL):
                ins = pe.matmul((ps_m, ps_s)[c][:, 0:T], ones, head[:, k, :], start=k == 0, stop=k == KL - 1)
            ins.then_inc(ms_ready, 1)

        for m in range(2 * KL + 1):
            full(Tile(T_LAT + m), a_hi, a_lo)
            if m == 0:
                transposes(HEADS - 1)
            if m == 1:
                pv(HEADS - 1)
            if m in (KL, 2 * KL):
                square_sums(m // KL - 1)
        with pe.Fori(0, KD // 2) as i:
            for b in range(2):
                full(Tile(T_GB + b, i, 2), a_hi, a_lo)
        pe.wait_ge(c_lo_r, 2)
        pe.wait_ge(kr_ready, 1)
        pe.wait_ge(o_lo, HEADS + 1)

        def head_b(h, first, a):
            t = Tile(T_MLA, h, 2) if not first else Tile(T_MLA)
            up_proj(t)
            if not first:
                transposes(a - 1)
            t = t.next()
            full(t, b_hi, b_lo)
            if not first:
                pv(a - 1)
            pe.wait_ge(rope_q, a - (HEADS - 1))
            pe.wait_ge(ev_v, a - (HEADS - 1))
            turn_v()
            scores(True)

        head_b(0, True, HEADS)
        with pe.Fori(1, HEADS) as h:
            head_b(h, False, h + HEADS)
        transposes(2 * HEADS - 1)
        pv(2 * HEADS - 1)
        pe.wait_ge(o_lo, 2 * HEADS + 1)
        with pe.Fori(0, KD // 2) as i:
            for b in range(2):
                full(Tile(T_MO + b, i, 2), a_hi, a_lo)
        pe.wait_ge(mix_lo, KD)
        with pe.Fori(0, KD // 2) as i:
            for b in range(2):
                full(Tile(T_WO + b, i, 2), b_hi, b_lo)
        pe.wait_ge(sum_ready, KD)
        for b in range(2):
            ins = pe.matmul(ps_m[:, 0:T], ones, run[:, b, :], start=b == 0, stop=b == 1)
        ins.then_inc(mean_ready, 1)
        for k in range(KD):
            if k % 4 == 0:
                pe.wait_ge(csq_ready, k // 4 + 1)
            ins = pe.matmul(ps_s[:, 0:T], ones, gate_a[:, k, :], start=k == 0, stop=k == KD - 1)
        ins.then_inc(mean_ready, 1)
        for b in range(2):
            full(Tile(T_WQ + b), a_hi, a_lo, h1_lo if b == 0 else None)
        with pe.Fori(1, KD // 2) as i:
            for b in range(2):
                full(Tile(T_WQ + b, i, 2), a_hi, a_lo)
        for b in range(2):
            pe.wait_ge(acc_free[(T_WQ + KD - 1 - b) % 2], (T_WQ + KD - 1 - b) // 2 + 2)
        pe.wait_ge(keys_in, 16)
        for g in range(8):
            tt, c0 = g // 4, 4 * (g % 4)
            if g >= 4:
                pe.wait_ge(sc_ready, g - 3)
            for c in range(4):
                ins = pe.matmul(spare[g % 4][:, P * c:P * c + P], qp[:, c0 + c, P * tt:P * tt + P], keys[:, (c0 + c) % 2, :],
                                start=True, stop=True)
            ins.then_inc(sc_mm, 1)
        for g in range(8):
            tt, c0 = g // 4, 4 * (g % 4)
            pe.wait_ge(sc_ready, g + 5) if g < 4 else pe.wait_ge(ht_ready, g - 3)
            pe.wait_ge(h1_ready, KD)
            for c in range(4):
                ins = pe.transpose(spare[g % 4][:, P * c:P * c + P], res[:, c0 + c, P * tt:P * tt + P], ident)
            ins.then_inc(ht_mm, 1)

        with pe.Fori(0, ROUNDS_TOP) as i:
            for b in range(8):
                full(Tile(T_DN + b, i, 8), a_hi, a_lo)
        pe.wait_ge(slots_ready, 2 * PEER_HEADS)
        pe.wait_ge(ht_ready, 8)
        for k in range(3):
            for tt in range(TT):
                ins = pe.transpose(spare[k][:, P * tt:P * tt + P], slot[:, k, tt, :], ident)
            ins.then_inc(st_mm, 1)
        with pe.Fori(0, TT * P // 64) as i:
            for b in range(16):
                full(Tile(T_DN + 8 * ROUNDS_TOP + b, i, 16), a_hi, a_lo)
                pe.wait_ge(oh_ready, i * 16 + (b + 1))
                pe.wait_ge(g_sb, i * 16 + (b + 1))
                for q in range(4):
                    ins = pe.matmul(ps_m[:, P * q:P * q + P], oh1[:, b % 2, q, :], oh2[:, b % 2, q, :], start=True, stop=True)
                ins.then_inc(g_mm, 1)
        with pe.Fori(0, ROUNDS_REST) as i:
            for b in range(8):
                full(Tile(T_DN + NKEYS - 8 * ROUNDS_REST + b, i, 8), a_hi, a_lo)

        pe.wait_ge(z_ready, 1)
        for t in (Tile(T_UP - 2), Tile(T_UP - 1)):
            pe.wait_ge(acc_free[t.par], t.pair + 2)
        for c in range(8):
            pe.matmul(ps[:, 512 * c:512 * c + 512], zero[:, 0:P], zero[:], start=True, stop=False, skip_group_check=True)

        def up(t, n, b):
            pe.wait_ge(mlo_ready, n + 1)
            for hf in range(2):
                half_ready(t, hf)
                for tt in range(TT):
                    s = slice(P * tt, P * tt + P)
                    for m, w in ((m_hi, w_hi), (m_hi, w_lo), (m_lo, w_hi)):
                        for c in range(2):
                            o = D * tt + HALF * hf + 512 * c
                            ins = pe.matmul(ps[:, o:o + 512], m[:, b % 2, s], w[:, t.slot(hf), 512 * c:512 * c + 512],
                                            start=False, stop=False, skip_group_check=True)
                ins.then_inc(half_used, 1)

        with pe.Fori(0, NKEYS // 8) as i:
            for b in range(8):
                up(Tile(T_UP + b, i, 8), i * 8 + b, b)

    ctx.close()


def _constants():
    c = np.zeros((P, N_CONST), np.float32)
    for b, (qt, kt) in enumerate(((0, 0), (1, 0), (1, 1))):
        q = np.arange(P)[:, None] + P * qt
        k = np.arange(P)[None, :] + P * kt
        d = q - k
        count = np.zeros((P, P), np.float32)
        for window, dilation in PATTERNS:
            count += (d >= 0) & (d <= window) & (d % dilation == 0)
        s = slice(P * b, P * b + P)
        c[:, C_D:][:, s] = -d
        c[:, C_NA:][:, s] = np.where(count > 0, 0.0, NEG)
        c[:, C_NB:][:, s] = np.where(d >= 0, 0.0, NEG)
        c[:, C_C:][:, s] = count
    half = ROPE // 2
    inv_freq = np.float32(10000.0) ** (-np.arange(half, dtype=np.float32) / np.float32(half))
    ang = (np.arange(T, dtype=np.float32)[:, None] * inv_freq[None, :]).T
    cos, sin = np.cos(ang), np.sin(ang)
    c[:, C_ROPE:C_ROPE + T] = np.concatenate([cos, cos, -sin, sin])
    c[:, C_ID:C_ID + P] = np.eye(P)
    c[:, C_ONE:C_ONE + P] = 1.0
    c[:, C_IOTA:C_IOTA + P] = np.arange(P)
    c[:, C_SLOPE:C_SLOPE + HEADS] = 2.0 ** (-8.0 * np.arange(1, HEADS + 1) / HEADS)
    return c


def _columns(w):
    return w.reshape(KD, P, -1, P).transpose(2, 1, 0, 3).reshape(-1, P, D)


def _rotary(w):
    t1, t2 = w[..., :ROPE // 2], w[..., ROPE // 2:]
    return np.concatenate([t1, t2, t2, t1], axis=-1)


def _stream(w_in, a_w_out, mla_w_uq, mla_w_ukv, mla_w_out, w_out, w_query, down, up):
    width = HEADS * P
    q, k, v, gate_a, gate_b = (_columns(w) for w in (
        w_in[:, :width], w_in[:, width:2 * width], w_in[:, 2 * width:3 * width], w_in[:, -2 * D:-D], w_in[:, -D:]))
    qkvg = np.stack([q, k, v, gate_a], axis=1).reshape(-1, P, D)
    latents = _columns(w_in[:, 3 * width:3 * width + 2 * LORA])
    rope = _columns(_rotary(w_in[:, 3 * width + 2 * LORA:-2 * D]))
    uq = mla_w_uq.reshape(KL, P, HEADS, NOPE + ROPE)
    ukv = mla_w_ukv.reshape(KL, P, HEADS, 2 * P)
    heads = np.stack([uq[..., :NOPE], _rotary(uq[..., NOPE:]), ukv[..., :P], ukv[..., P:]])
    heads = heads.transpose(3, 2, 0, 1, 4).reshape(HEADS, P, D)
    mla = np.stack([heads, _columns(a_w_out)], axis=1).reshape(-1, P, D)
    dn = down.reshape(NKEYS, NKEYS, KD, P).transpose(1, 3, 2, 0).reshape(NKEYS, P, D)
    upt = up.reshape(NKEYS, NKEYS, D).transpose(1, 0, 2)
    s = np.concatenate([qkvg, latents, rope, gate_b, mla, _columns(mla_w_out), _columns(w_out), _columns(w_query), dn, upt])
    return s.reshape(N_TILES, P, 2, HALF).transpose(0, 2, 1, 3).reshape(2 * N_TILES, P, HALF)


def kernel(**inputs):
    import concourse.bacc as bacc
    from concourse.bass_utils import run_bass_kernel_spmd

    v = {n: np.asarray(a)[0] for n, a in inputs.items()}
    arrays = {
        "stream": np.ascontiguousarray(_stream(
            v["w_in"], v["a_w_out"], v["mla_w_uq"], v["mla_w_ukv"], v["mla_w_out"], v["w_out"], v["peer_w_query"],
            v["peer_expert_down"], v["peer_expert_up"])),
        "x_t": np.ascontiguousarray(v["x"].reshape(T, KD, P).transpose(2, 1, 0)),
        "const_in": _constants(),
        "small_in": np.ascontiguousarray(np.concatenate([
            v[n].reshape(-1, P) for n in ("b_gates", "mla_q_norm", "mla_kv_norm", "ln1_g", "ln1_b")]).T),
        "keys_t": np.ascontiguousarray(np.stack([v["peer_sub_keys_1"].T, v["peer_sub_keys_2"].T], axis=1)),
        "ln2": np.stack([v["ln2_g"], v["ln2_b"]]),
    }
    nc = bacc.Bacc("TRN2", target_bir_lowering=False, num_devices=1)
    args = [nc.dram_tensor(n, a.shape, mybir.dt.from_np(a.dtype), kind="ExternalInput").ap() for n, a in arrays.items()]
    args.append(nc.dram_tensor("y_out", (TT, P, D), F32, kind="ExternalOutput").ap())
    args.append(nc.dram_tensor("a_dram", (NKEYS // 4, P, 4, T), F32).ap())
    args.append(nc.dram_tensor("g_dram", (T // 32, P, NKEYS * 32), F32).ap())
    build(nc, *args)
    r = run_bass_kernel_spmd(nc, [arrays], core_ids=[0])
    return r.results[0]["y_out"].reshape(1, T, D)
```
